# Optimizing a Trainium2 kernel written in Bass

```python
import jax, jax.numpy as jnp
from jax import lax
import numpy as np

D_MODEL = 1024
BATCH = 1
SEQ = 256
DEPTH = 1
DEC_BATCH = 8
DEC_SEQ = 4
PAST_LEN = 2048
PAGE_SIZE = 128

HEAD_DIM = 64
D_MIX = D_MODEL
N_HEADS_A = 6
N_HEADS_B = 6
N_GROUPS_C = 4
D_A = N_HEADS_A * HEAD_DIM
D_B = N_HEADS_B * HEAD_DIM
D_C = D_MIX - D_A - D_B
C_GROUP = D_C // N_GROUPS_C
POOL_WINDOWS = (2, 4, 8, 16)
POOL_BUF = max(POOL_WINDOWS) - 1
CONV_A = 3
CONV_B = 31
D_IN = 3 * D_A + 2 * D_B + D_C
IN_SPLITS = (D_A, 2 * D_A, 3 * D_A, 3 * D_A + D_B, 3 * D_A + 2 * D_B)
N_EXPERTS = 64
TOP_K = 8
N_EXPERT_GROUPS = 8
TOPK_GROUPS = 4
D_EXPERT = 256
D_SHARED = 256
ROUTED_SCALE = 2.5
N_MOD = 6
EPS = 1e-6

kernel_name = 'hybrid_conv_pool_moe_adaln_decode_step'

def rms_norm(x, g):
    xf = x.astype(jnp.float32)
    y = xf * lax.rsqrt(jnp.mean(xf * xf, axis=-1, keepdims=True) + EPS)
    return (y * g.astype(jnp.float32)).astype(x.dtype)

def layer_norm(x, g, b):
    xf = x.astype(jnp.float32)
    mu = jnp.mean(xf, axis=-1, keepdims=True)
    var = jnp.mean(jnp.square(xf - mu), axis=-1, keepdims=True)
    y = (xf - mu) * lax.rsqrt(var + EPS)
    return (y * g.astype(jnp.float32) + b.astype(jnp.float32)).astype(x.dtype)

def causal_depthwise_conv(buf, u, w):
    xx = jnp.concatenate([buf.astype(u.dtype), u], axis=1)
    k = w.shape[0]
    out = lax.conv_general_dilated(xx, w[:, None, :].astype(u.dtype), window_strides=(1,), padding='VALID',
                                   dimension_numbers=('NWC', 'WIO', 'NWC'), feature_group_count=u.shape[-1])
    return out, xx[:, xx.shape[1] - (k - 1):, :]

def short_conv_mixer(xa, ca, ba, buf, w):
    v, new_buf = causal_depthwise_conv(buf, ca * xa, w)
    return ba * v, new_buf

def conformer_conv_mixer(a, g, buf, w, bias, ln_g, ln_b):
    u = a * jax.nn.sigmoid(g)
    v, new_buf = causal_depthwise_conv(buf, u, w)
    v = layer_norm(v + bias.astype(v.dtype), ln_g, ln_b)
    return jax.nn.silu(v), new_buf

def multiscale_pool_mixer(p, buf, pos, w_pool, scale):
    n, t, _ = p.shape
    xx = jnp.concatenate([buf.astype(p.dtype), p], axis=1)
    xf = xx.astype(jnp.float32)
    cs = jnp.concatenate([jnp.zeros_like(xf[:, :1]), jnp.cumsum(xf, axis=1)], axis=1)
    cur = cs[:, POOL_BUF + 1:]
    pooled = []
    for gi, win in enumerate(POOL_WINDOWS):
        lo, hi = gi * C_GROUP, (gi + 1) * C_GROUP
        start = POOL_BUF + 1 - win
        wsum = cur[..., lo:hi] - cs[:, start:start + t, lo:hi]
        cnt = jnp.minimum(pos + 1, win).astype(jnp.float32)[None, :, None]
        pooled.append(wsum / cnt)
    d = jnp.concatenate(pooled, axis=-1) - p.astype(jnp.float32)
    d = d.reshape(n, t, N_GROUPS_C, C_GROUP)
    y = jnp.einsum('btgc,gcd->btgd', d, w_pool.astype(jnp.float32)).reshape(n, t, D_C)
    return (y * scale.astype(jnp.float32)).astype(p.dtype), xx[:, xx.shape[1] - POOL_BUF:, :]

def moe_ffn(h, w_router, router_bias, w_gate, w_up, w_down, ws_gate, ws_up, ws_down):
    lead = h.shape[:-1]
    x = h.reshape(-1, D_MODEL)
    t = x.shape[0]
    rows = jnp.arange(t)[:, None]
    scores = jax.nn.sigmoid(jnp.dot(x.astype(jnp.float32), w_router.astype(jnp.float32)))
    biased = scores + router_bias.astype(jnp.float32)
    grp = biased.reshape(t, N_EXPERT_GROUPS, N_EXPERTS // N_EXPERT_GROUPS)
    grp_score = jnp.sum(lax.top_k(grp, 2)[0], axis=-1)
    _, grp_idx = lax.top_k(grp_score, TOPK_GROUPS)
    grp_mask = jnp.zeros((t, N_EXPERT_GROUPS), bool).at[rows, grp_idx].set(True)
    expert_mask = jnp.repeat(grp_mask, N_EXPERTS // N_EXPERT_GROUPS, axis=1)
    _, idx = lax.top_k(jnp.where(expert_mask, biased, -jnp.inf), TOP_K)
    sel = jnp.take_along_axis(scores, idx, axis=-1)
    wts = sel / jnp.sum(sel, axis=-1, keepdims=True) * ROUTED_SCALE
    gates = jnp.zeros((t, N_EXPERTS), jnp.float32).at[rows, idx].set(wts).astype(x.dtype)

    def expert_step(acc, ew):
        wg, wu, wd, g = ew
        hid = jax.nn.silu(x @ wg) * (x @ wu)
        return acc + (g[:, None] * (hid @ wd)).astype(acc.dtype), None

    routed, _ = lax.scan(expert_step, jnp.zeros_like(x), (w_gate, w_up, w_down, gates.T))
    shared = (jax.nn.silu(x @ ws_gate) * (x @ ws_up)) @ ws_down
    return (routed + shared).reshape(*lead, D_MODEL)

def decoder_layer(x, c, pos, buf_a, buf_b, buf_c, w_ada, b_ada, norm_mix_g, w_in, conv_a_w, conv_b_w,
                  conv_b_bias, ln_b_g, ln_b_b, pool_w, pool_scale, w_out, norm_ffn_g, w_router,
                  router_bias, w_gate, w_up, w_down, ws_gate, ws_up, ws_down):
    mod = (jax.nn.silu(c) @ w_ada + b_ada).astype(x.dtype)
    sh_m, sc_m, g_m, sh_f, sc_f, g_f = jnp.split(mod[:, None, :], N_MOD, axis=-1)
    h = rms_norm(x, norm_mix_g) * (1 + sc_m) + sh_m
    proj = h @ w_in
    xa, ca, ba, a_b, g_b, p_c = jnp.split(proj, IN_SPLITS, axis=-1)
    ya, na = short_conv_mixer(xa, ca, ba, buf_a, conv_a_w)
    yb, nb = conformer_conv_mixer(a_b, g_b, buf_b, conv_b_w, conv_b_bias, ln_b_g, ln_b_b)
    yc, nc = multiscale_pool_mixer(p_c, buf_c, pos, pool_w, pool_scale)
    x = x + g_m * (jnp.concatenate([ya, yb, yc], axis=-1) @ w_out)
    h = rms_norm(x, norm_ffn_g) * (1 + sc_f) + sh_f
    x = x + g_f * moe_ffn(h, w_router, router_bias, w_gate, w_up, w_down, ws_gate, ws_up, ws_down)
    return x, na, nb, nc

def run_trunk(x, c, pos, buf_a, buf_b, buf_c, params, final_norm_g):
    new_a, new_b, new_c = [], [], []
    for l in range(DEPTH):
        layer_params = tuple(p[l] for p in params)
        x, na, nb, nc = decoder_layer(x, c, pos, buf_a[l], buf_b[l], buf_c[l], *layer_params)
        new_a.append(na)
        new_b.append(nb)
        new_c.append(nc)
    return rms_norm(x, final_norm_g), jnp.stack(new_a), jnp.stack(new_b), jnp.stack(new_c)

def setup_inputs(seed: int = 0) -> dict:
    key = jax.random.key(seed)
    ks = iter(jax.random.split(key, 40))

    def nrm(shape, s):
        return jax.random.normal(next(ks), shape, jnp.float32) * s

    L = DEPTH
    return {
        'x_prompt': nrm((BATCH, SEQ, D_MODEL), 1.0),
        'x_sample': nrm((DEC_BATCH, DEC_SEQ, D_MODEL), 1.0),
        'c_prompt': nrm((BATCH, D_MODEL), 1.0),
        'c_sample': nrm((DEC_BATCH, D_MODEL), 1.0),
        'state_conv_a': nrm((L, DEC_BATCH, CONV_A - 1, D_A), 1.0),
        'state_conv_b': nrm((L, DEC_BATCH, CONV_B - 1, D_B), 1.0),
        'state_pool': nrm((L, DEC_BATCH, POOL_BUF, D_C), 1.0),
        'w_ada': nrm((L, D_MODEL, N_MOD * D_MODEL), 0.5 * D_MODEL ** -0.5),
        'b_ada': nrm((L, N_MOD * D_MODEL), 0.02),
        'norm_mix_g': 1.0 + nrm((L, D_MODEL), 0.02),
        'w_in': nrm((L, D_MODEL, D_IN), D_MODEL ** -0.5),
        'conv_a_w': nrm((L, CONV_A, D_A), CONV_A ** -0.5),
        'conv_b_w': nrm((L, CONV_B, D_B), CONV_B ** -0.5),
        'conv_b_bias': nrm((L, D_B), 0.02),
        'ln_b_g': 1.0 + nrm((L, D_B), 0.02),
        'ln_b_b': nrm((L, D_B), 0.02),
        'pool_w': nrm((L, N_GROUPS_C, C_GROUP, C_GROUP), C_GROUP ** -0.5),
        'pool_scale': 1.0 + nrm((L, D_C), 0.1),
        'w_out': nrm((L, D_MIX, D_MODEL), D_MIX ** -0.5),
        'norm_ffn_g': 1.0 + nrm((L, D_MODEL), 0.02),
        'w_router': nrm((L, D_MODEL, N_EXPERTS), D_MODEL ** -0.5),
        'router_bias': nrm((L, N_EXPERTS), 0.01),
        'w_gate': nrm((L, N_EXPERTS, D_MODEL, D_EXPERT), D_MODEL ** -0.5),
        'w_up': nrm((L, N_EXPERTS, D_MODEL, D_EXPERT), D_MODEL ** -0.5),
        'w_down': nrm((L, N_EXPERTS, D_EXPERT, D_MODEL), D_EXPERT ** -0.5),
        'ws_gate': nrm((L, D_MODEL, D_SHARED), D_MODEL ** -0.5),
        'ws_up': nrm((L, D_MODEL, D_SHARED), D_MODEL ** -0.5),
        'ws_down': nrm((L, D_SHARED, D_MODEL), D_SHARED ** -0.5),
        'final_norm_g': 1.0 + nrm((D_MODEL,), 0.02),
    }

def reference(x_prompt, x_sample, c_prompt, c_sample, state_conv_a, state_conv_b, state_pool,
              w_ada, b_ada, norm_mix_g, w_in, conv_a_w, conv_b_w, conv_b_bias, ln_b_g, ln_b_b,
              pool_w, pool_scale, w_out, norm_ffn_g, w_router, router_bias,
              w_gate, w_up, w_down, ws_gate, ws_up, ws_down, final_norm_g):
    params = (w_ada, b_ada, norm_mix_g, w_in, conv_a_w, conv_b_w, conv_b_bias, ln_b_g, ln_b_b,
              pool_w, pool_scale, w_out, norm_ffn_g, w_router, router_bias,
              w_gate, w_up, w_down, ws_gate, ws_up, ws_down)
    n_p = x_prompt.shape[0]
    pos_prompt = jnp.arange(x_prompt.shape[1], dtype=jnp.int32)
    pos_sample = PAST_LEN + jnp.arange(x_sample.shape[1], dtype=jnp.int32)
    zero_a = jnp.zeros((DEPTH, n_p, CONV_A - 1, D_A), x_prompt.dtype)
    zero_b = jnp.zeros((DEPTH, n_p, CONV_B - 1, D_B), x_prompt.dtype)
    zero_c = jnp.zeros((DEPTH, n_p, POOL_BUF, D_C), x_prompt.dtype)
    y_prompt, na_p, nb_p, nc_p = run_trunk(x_prompt, c_prompt, pos_prompt, zero_a, zero_b, zero_c,
                                           params, final_norm_g)
    y_sample, na_s, nb_s, nc_s = run_trunk(x_sample, c_sample, pos_sample, state_conv_a, state_conv_b,
                                           state_pool, params, final_norm_g)
    return (y_prompt, y_sample, na_p, nb_p, nc_p, na_s, nb_s, nc_s)


_drawn_inputs = setup_inputs


def setup_inputs(seed=0):
    import zlib

    import numpy as np

    out = dict(_drawn_inputs(seed))
    spreads = {}
    factors = {'conv_b_bias': 3.368,
     'ln_b_g': 31.863,
     'ln_b_b': 27.723,
     'final_norm_g': 20.378,
     'pool_scale': 5.577,
     'norm_ffn_g': 3.841,
     'router_bias': 2.67}
    for name, (base, spread) in spreads.items():
        noise = np.random.default_rng([zlib.crc32(name.encode()), seed]).standard_normal(out[name].shape)
        drawn = base * np.exp(spread * noise) if base else spread * noise
        out[name] = __import__('jax').numpy.asarray(drawn.astype(out[name].dtype))
    for name, factor in factors.items():
        out[name] = (out[name] * factor).astype(out[name].dtype)
    return out
```

```python
from contextlib import ExitStack

import concourse.bass as bass
from concourse import mybir

F32 = mybir.dt.float32
F32R = mybir.dt.float32r
ALU = mybir.AluOpType
ACT = mybir.ActivationFunctionType
AX_X = mybir.AxisListType.X

P = 128
D = 1024
C = D // P
SEQ, NSEQ, STEPS = 256, 8, 4
NS = NSEQ * STEPS
T = SEQ + NS
TT = 96
NT = T // TT
DA, DB, DC = 384, 384, 256
CA, CB, CC = DA // P, DB // P, DC // P
KA, KB, KP = 3, 31, 16
SA, SB, SP = KA - 1, KB - 1, KP - 1
WA, WB, WP = SA + SEQ, SB + SEQ, SP + SEQ
LA, LB, LP = SA + STEPS, SB + STEPS, SP + STEPS
WINDOWS = (2, 4, 8, 16)
E, F = 64, 256
GROUPS, TOPG = 8, 4
FC = F // P
EPS = 1e-6
SCALE = 2.5
BIG = 1e30
N_SEQ_ALL = NSEQ + 1


class Jobs:

    def __init__(self):
        self.names, self.bank, self.reader = [], {}, {}

    def add(self, name, bank, reader):
        self.names.append(name)
        self.bank[name], self.reader[name] = bank, reader

    def full(self, name):
        return self.names.index(name) + 1

    def read(self, name):
        mine = [n for n in self.names if self.reader[n] == self.reader[name]]
        return mine.index(name) + 1

    def before(self, name):
        i = self.names.index(name)
        for n in reversed(self.names[:i]):
            if self.bank[n] == self.bank[name]:
                return n
        return None


def plan_jobs():
    j = Jobs()
    small, big = [0], [0]

    def s(name, reader):
        j.add(name, small[0] % 2, reader)
        small[0] += 1

    def b(name, reader):
        j.add(name, 2 + big[0] % 6, reader)
        big[0] += 1

    s("cT", "dve")
    for c in range(C):
        b(f"x{c}", "act")
    s("vec", "dve")
    s("hist_a", "dve")
    s("hist_b0", "dve")
    s("hist_b1", "dve")
    s("hist_p", "dve")
    s("mod1", "dve")
    s("mod0", "dve")
    s("rms1", "dve")
    for m in range(CB):
        b(f"gb{m}", "act")
        b(f"ab{m}", "dve")
    s("mod2", "dve")
    for m in range(CA):
        b(f"xa{m}", "act")
        b(f"ca{m}", "act")
        b(f"ba{m}", "act")
    s("mod3", "dve")
    for m in range(CC):
        b(f"pc{m}", "act")
    s("mod4", "dve")
    s("mod5", "dve")
    for k in ("new_a_prompt", "new_a_sample", "new_b_prompt", "new_b_sample", "new_p_prompt", "new_p_sample"):
        b(k, "act")
    for m in range(CC):
        b(f"pool{m}", "dve")
    s("ln_sum", "dve")
    s("ln_var", "dve")
    for c in range(C):
        b(f"out{c}", "dve")
    s("rms2", "dve")
    s("router", "act")
    j.add("gatesT", 4, "dve")
    return j


def layer(nc, x_prompt, x_sample, c_prompt, c_sample, state_a, state_b, state_p, w_ada, b_ada, norm_mix_g,
          w_in, conv_a_w, conv_b_w, conv_b_bias, ln_b_g, ln_b_b, pool_w, pool_scale, w_out, norm_ffn_g,
          w_router, router_bias, w_gate, w_up, w_down, ws_gate, ws_up, ws_down, final_norm_g,
          y_prompt, y_sample, na_p, nb_p, np_p, na_s, nb_s, np_s):
    J = plan_jobs()
    with ExitStack() as ctx:
        ctx.enter_context(nc.allow_non_contiguous_dma(reason="small vectors and state rows"))
        base = (nc.sbuf_base + 63) // 64 * 64

        def at(kb, name, shape, dt=F32):
            size = 4
            for k in shape[1:]:
                size *= k
            assert base + int(kb * 1024) + size <= nc.sbuf_top, name
            return nc.alloc_sbuf_tensor_at(name, shape, dt, offset=base + int(kb * 1024))

        def sem(name):
            return ctx.enter_context(nc.semaphore(name))

        g_hi = at(0, "g_hi", [P, 2, C, F], F32R)
        g_lo = at(16, "g_lo", [P, 2, C, F], F32R)
        u_hi = at(32, "u_hi", [P, 2, C, F], F32R)
        u_lo = at(48, "u_lo", [P, 2, C, F], F32R)
        d_hi = at(64, "d_hi", [P, FC, D], F32R)
        d_lo = at(72, "d_lo", [P, FC, D], F32R)
        g_raw = at(80, "g_raw", [P, 2, C, F])
        u_raw = at(96, "u_raw", [P, 2, C, F])
        d_raw = at(112, "d_raw", [P, 2, FC, D])
        h_hi = at(128, "h_hi", [P, C, T], F32R)
        h_lo = at(137, "h_lo", [P, C, T], F32R)
        acc = at(146, "acc", [P, C, T])
        xT = at(155, "xT", [P, C, T])
        hT = at(164, "hT", [P, C, T])
        sil = at(173, "sil", [P, FC, T])
        prod = at(175.25, "prod", [P, FC, T])
        hid = at(177.5, "hid", [P, FC, T])
        hid_hi = at(179.75, "hid_hi", [P, FC, T], F32R)
        hid_lo = at(182, "hid_lo", [P, FC, T], F32R)
        gatesT = at(184.25, "gatesT", [E, T])
        gate_row = at(185.5, "gate_row", [E, 2, T])
        w_in_sb = at(0, "w_in_sb", [P, C, 3 * DA + 2 * DB + DC])
        x_tok = at(68.25, "x_tok", [TT, NT, D])
        ada = [at(81, "ada0", [P, C, D]), at(113, "ada1", [P, C, D])]
        w_out_sb = at(113, "w_out_sb", [P, C, D])
        cat = at(146, "cat", [P, C, T])
        sq1 = at(146, "sq1", [P, C, T])
        sq2 = at(128, "sq2", [P, C, T])
        ua = at(173, "ua", [P, CA, WA + NSEQ * LA])
        ba = at(176.75, "ba", [P, CA, T])
        ub = at(180.25, "ub", [P, CB, WB + NSEQ * LB])
        pc = at(187, "pc", [P, CC, WP + NSEQ * LP])
        vb = at(190.5, "vb", [P, CB, T])
        win2 = at(68.25, "win2", [P, WP + NSEQ * LP])
        win4 = at(70, "win4", [P, WP + NSEQ * LP])
        win8 = at(71.75, "win8", [P, WP + NSEQ * LP])
        va = at(73.5, "va", [P, CA, T])
        diff = at(77.125, "diff", [P, CC, T])
        sig = at(79.5, "sig", [P, T])
        ln_sq_t = at(180.25, "ln_sq_t", [P, CB, T])
        xa = at(137, "xa", [P, CA, T])
        ca = at(141, "ca", [P, CA, T])
        mod = at(194, "mod", [P, 6, C, N_SEQ_ALL])
        ident = at(195.75, "ident", [P, P])
        ones = at(196.25, "ones", [P, P])
        rstd = at(196.75, "rstd", [P, T])
        gmul = at(198, "gmul", [P, C, N_SEQ_ALL])
        smallv = at(198.375, "smallv", [P, 3, C])
        vecs = at(198.5, "vecs", [P, 3, 38])
        badaT = at(199, "badaT", [P, 6, C])
        pw = at(199.25, "pw", [P, CC, P])
        tmps = at(200.5, "tmps", [P, C, NSEQ, STEPS])
        steps = at(200.5, "steps", [P, C, NS])
        invc = at(201.5, "invc", [P, CC, KP])
        cT = at(201.75, "cT", [P, C, N_SEQ_ALL])
        rows = at(81, "rows", [38, DA])
        hist_a = at(82.5, "hist_a", [NSEQ * SA, DA])
        hist_b = at(84, "hist_b", [4 * SB, 2, DB])
        hist_p = at(87, "hist_p", [NSEQ * SP, DC])
        c_tok = at(88, "c_tok", [N_SEQ_ALL, D])
        c_sil = at(92, "c_sil", [N_SEQ_ALL, D])
        new_rows = at(164, "new_rows", [NS, 6, DA])
        w_rt = at(202.25, "w_rt", [P, C, E])
        bias_rt = at(204.25, "bias_rt", [TT, E])
        lower = at(204.5, "lower", [TT, GROUPS, GROUPS])
        top8 = at(204.75, "top8", [TT, NT, 8])
        gsum = at(204.875, "gsum", [TT, 2, NT])
        gs = at(205, "gs", [TT, 4, NT * GROUPS])
        pair = at(205.5, "pair", [TT, NT * GROUPS, GROUPS])
        pair2 = at(206.25, "pair2", [TT, NT * GROUPS, GROUPS])
        score = at(188, "score", [TT, NT, E])
        biased = at(188.75, "biased", [TT, NT, E])
        rt_a = at(189.5, "rt_a", [TT, NT, E])
        rt_b = at(190.25, "rt_b", [TT, NT, E])
        gates = at(191, "gates", [TT, NT, E])
        iota_i = at(207, "iota_i", [P, KP], mybir.dt.int32)
        y_tok = at(0, "y_tok", [TT, NT, D])
        yT = at(16, "yT", [P, C, T])
        sqT = at(32, "sqT", [P, C, T])

        bank = [ctx.enter_context(nc.psum_tensor(f"bank{i}", [P, 512], F32)) for i in range(4, 8)]
        gu_ps = ctx.enter_context(nc.psum_tensor("gu_ps", [P, 4, 512], F32))
        bank = [gu_ps[:, i, :] for i in range(4)] + [b[:, :] for b in bank]

        def tile(name):
            return bank[J.bank[name]]

        psum_full = sem("psum_full")
        act_read = sem("act_read")
        dve_read = sem("dve_read")
        c_in, x_in, rows_in, hist_in = sem("c_in"), sem("x_in"), sem("rows_in"), sem("hist_in")
        smallv_in, bada_in, pw_in, router_in = sem("smallv_in"), sem("bada_in"), sem("pw_in"), sem("router_in")
        ada_in = [sem("ada_in0"), sem("ada_in1")]
        win_in = [sem("win_in_b"), sem("win_in_a"), sem("win_in_c")]
        wout_in = sem("wout_in")
        state_out = sem("state_out")
        y_out = sem("y_out")
        ident_z, consts = sem("ident_z"), sem("consts")
        pads, pw_z = sem("pads"), sem("pw_z")
        c_silu = sem("c_silu")
        vstep = sem("vstep")
        root = [sem("root1"), sem("root2"), sem("root3")]
        pool_step = sem("pool_step")
        steps_ready = sem("steps_ready")
        ua_done, win_done = sem("ua_done"), sem("win_done")
        sq_ready = [sem("sq_ready1"), sem("sq_ready2"), sem("sq_ready3")]
        xn_ready = [sem("xn_ready1"), sem("xn_ready2")]
        h_prompt, h_sample = [sem("h_prompt1"), sem("h_prompt2")], [sem("h_sample1"), sem("h_sample2")]
        ub_ready = sem("ub_ready")
        ln_rt, lnn = sem("ln_rt"), sem("lnn")
        ln_mean, ln_sq_ready = sem("ln_mean"), sem("ln_sq_ready")
        cat_a, cat_b = sem("cat_a"), sem("cat_b")
        diff_ready = sem("diff_ready")
        gates_ready = sem("gates_ready")
        h_hi_ready, h_lo_ready = sem("h_hi_ready"), sem("h_lo_ready")
        shared_gate = sem("shared_gate")
        lowmask = sem("lowmask")
        raw_in = {(k, s): sem(f"{k}_in{s}") for k in "gud" for s in range(2)}
        hi_done = {k: sem(f"{k}_hi_done") for k in "gud"}
        lo_done = {k: sem(f"{k}_lo_done") for k in "gud"}
        gu_done = sem("gu_done")
        gate_row_done = sem("gate_row_done")
        gate_bc_done = sem("gate_bc_done")
        silu_done = sem("silu_done")
        up_done = sem("up_done")
        hid_done = sem("hid_done")
        hid_hi_done, hid_lo_done = sem("hid_hi_done"), sem("hid_lo_done")
        down_full = sem("down_full")
        acc_added = sem("acc_added")
        x2_square, x2_mean = sem("x2_square"), sem("x2_mean")
        yn_ready, y_full, y_copied = sem("yn_ready"), sem("y_full"), sem("y_copied")

        GUCOL = {"g": (g_hi, g_lo, g_raw), "u": (u_hi, u_lo, u_raw)}
        block = ctx.enter_context(nc.Block())

        @block.sync
        def _(sp):
            sp.dma_start(c_tok[0:1, :], c_prompt).then_inc(c_in, 16)
            sp.dma_start(c_tok[1:N_SEQ_ALL, :], c_sample).then_inc(c_in, 16)
            xs = x_sample.rearrange("b t d -> (b t) d")
            sp.dma_start(x_tok[:, 0, :], x_prompt[0, 0:TT, :]).then_inc(x_in, 16)
            sp.dma_start(x_tok[:, 1, :], x_prompt[0, TT:2 * TT, :]).then_inc(x_in, 16)
            sp.dma_start(x_tok[0:SEQ - 2 * TT, 2, :], x_prompt[0, 2 * TT:SEQ, :]).then_inc(x_in, 16)
            sp.dma_start(x_tok[SEQ - 2 * TT:TT, 2, :], xs).then_inc(x_in, 16)

            def load_ada(order, group):
                slot = order % 2
                sp.dma_start(ada[slot][:, :, :],
                             w_ada[0, :, group * D:(group + 1) * D].rearrange("(c p) n -> p c n", p=P)
                             ).then_inc(ada_in[slot], 16)

            load_ada(1, 1)
            sp.wait_ge(psum_full, J.full("hist_p"))
            load_ada(0, 0)
            w_in_v = w_in[0].rearrange("(c p) n -> p c n", p=P)
            for i, (a, b) in enumerate(((3 * DA, 3 * DA + 2 * DB), (0, 3 * DA), (3 * DA + 2 * DB, 3 * DA + 2 * DB + DC))):
                sp.dma_start(w_in_sb[:, :, a:b], w_in_v[:, :, a:b]).then_inc(win_in[i], 16)
            sp.wait_ge(psum_full, J.full("mod1"))
            load_ada(1, 2)
            sp.wait_ge(psum_full, J.full("mod0"))
            load_ada(0, 3)
            sp.wait_ge(psum_full, J.full("mod2"))
            load_ada(1, 4)
            sp.wait_ge(psum_full, J.full("mod3"))
            load_ada(0, 5)
            sp.wait_ge(psum_full, J.full("mod4"))
            sp.dma_start(w_out_sb[:, :, :], w_out[0].rearrange("(c p) n -> p c n", p=P)).then_inc(wout_in, 16)
            sp.wait_ge(psum_full, J.full("mod5"))

            def load(kind, slot, src):
                dst = {"g": g_raw, "u": u_raw, "d": d_raw}[kind]
                sp.dma_start(dst[:, slot, :, :], src).then_inc(raw_in[kind, slot], 16)

            def expert(w, e):
                return w[0, bass.ds(e, 1)].rearrange("e (c p) n -> p (e c) n", p=P)

            load("g", 0, ws_gate[0].rearrange("(c p) n -> p c n", p=P))
            load("u", 0, ws_up[0].rearrange("(c p) n -> p c n", p=P))
            load("g", 1, expert(w_gate, 0))
            sp.wait_ge(psum_full, J.full(f"out{C - 1}"))
            load("u", 1, expert(w_up, 0))
            load("d", 0, ws_down[0].rearrange("(c p) n -> p c n", p=P))
            load("d", 1, expert(w_down, 0))

            def load_item(n, slot):
                for kind, w in (("g", w_gate), ("u", w_up), ("d", w_down)):
                    sp.wait_ge(lo_done[kind], n - 1)
                    load(kind, slot, expert(w, n - 1))

            with sp.Fori(0, (E - 2) // 2) as i:
                load_item(i * 2 + 2, 0)
                load_item(i * 2 + 3, 1)
            load_item(E, 0)
            sp.wait_ge(y_copied, 2 * NT)
            yp, ys = y_prompt[0], y_sample.rearrange("b t d -> (b t) d")
            sp.dma_start(yp[0:TT, :], y_tok[:, 0, :]).then_inc(y_out, 16)
            sp.dma_start(yp[TT:2 * TT, :], y_tok[:, 1, :]).then_inc(y_out, 16)
            sp.dma_start(yp[2 * TT:SEQ, :], y_tok[0:SEQ - 2 * TT, 2, :]).then_inc(y_out, 16)
            sp.dma_start(ys, y_tok[SEQ - 2 * TT:TT, 2, :]).then_inc(y_out, 16)
            sp.wait_ge(y_out, 64)
            sp.wait_ge(state_out, 16 * (5 + 3 * NSEQ))

        @block.gpsimd
        def _(pool):
            nc.gpsimd.memset(ident[:, :], 0.0).then_inc(ident_z, 1)
            nc.gpsimd.memset(ones[:, :], 1.0).then_inc(consts, 1)
            pool.wait_ge(ident_z, 1)
            nc.gpsimd.affine_select(out=ident[:, :], in_=ident[:, :], compare_op=ALU.not_equal, fill=1.0, base=0,
                                    pattern=[[-1, P]], channel_multiplier=1).then_inc(consts, 1)
            nc.gpsimd.memset(ua[:, :, 0:SA], 0.0).then_inc(pads, 1)
            nc.gpsimd.memset(ub[:, :, 0:SB], 0.0).then_inc(pads, 1)
            nc.gpsimd.memset(pc[:, :, 0:SP], 0.0).then_inc(pads, 1)
            nc.gpsimd.memset(pw[:, :, :], 0.0).then_inc(pw_z, 1)
            nc.gpsimd.iota(iota_i[:, :], pattern=[[1, KP]], base=1, channel_multiplier=0).then_inc(pads, 1)
            nc.gpsimd.memset(lower[:, :, :], 1.0).then_inc(lowmask, 1)
            pool.wait_ge(lowmask, 1)
            nc.gpsimd.affine_select(out=lower[:, :, :], in_=lower[:, :, :], compare_op=ALU.is_ge, fill=0.0, base=-1,
                                    pattern=[[1, GROUPS], [-1, GROUPS]], channel_multiplier=0).then_inc(lowmask, 1)
            for i, v in enumerate((norm_mix_g[0], norm_ffn_g[0], final_norm_g)):
                pool.dma_start(smallv[:, i, :], v.rearrange("(c p) -> p c", p=P)).then_inc(smallv_in, 16)
            pool.dma_start(badaT[:, :, :], b_ada[0].rearrange("(g c p) -> p g c", g=6, p=P)).then_inc(bada_in, 16)
            pool.wait_ge(pw_z, 1)
            for g in range(4):
                h = 64 * (g % 2)
                pool.dma_start(pw[h:h + 64, g // 2, h:h + 64], pool_w[0, g]).then_inc(pw_in, 16)
            pool.dma_start(w_rt[:, :, :], w_router[0].rearrange("(c p) n -> p c n", p=P)).then_inc(router_in, 16)
            pool.dma_start(bias_rt[:, :], router_bias.broadcast_to([TT, E])).then_inc(router_in, 16)
            pool.dma_start(nb_s[0, :, 0:SB - STEPS, :], state_b[0, :, STEPS:SB, :]).then_inc(state_out, 16)
            pool.dma_start(np_s[0, :, 0:SP - STEPS, :], state_p[0, :, STEPS:SP, :]).then_inc(state_out, 16)
            for m in range(CA):
                pool.wait_ge(act_read, J.read(f"ca{m}"))
                nc.gpsimd.tensor_tensor(ua[:, m, SA:WA], ua[:, m, SA:WA], cat[:, CA + m, 0:SEQ], ALU.mult).then_inc(ua_done, 1)
                v = ua[:, m, WA:].rearrange("p (b l) -> p b l", b=NSEQ)[:, :, SA:]
                nc.gpsimd.tensor_tensor(v, v, cat[:, CA + m, SEQ:T].rearrange("p (b l) -> p b l", b=NSEQ),
                                        ALU.mult).then_inc(ua_done, 1)
            pool.wait_ge(dve_read, J.read("hist_p"))
            pool.wait_ge(pads, 4)
            n_pool = [0]

            def pstep(ins):
                n_pool[0] += 1
                ins.then_inc(pool_step, 1)
                pool.wait_ge(pool_step, n_pool[0])

            LEN = WP + NSEQ * LP
            for m in range(CC):
                pool.wait_ge(act_read, J.read(f"pc{m}"))
                if m == 1:
                    pool.wait_ge(diff_ready, 1)
                    pool.wait_ge(win_done, 1)
                lo, hi = (0, 64), (64, P)
                pstep(nc.gpsimd.tensor_tensor(win2[:, 1:LEN], pc[:, m, 1:LEN], pc[:, m, 0:LEN - 1], ALU.add))
                if m == 0:
                    pstep(nc.gpsimd.tensor_tensor(win4[64:P, 3:LEN], win2[64:P, 3:LEN], win2[64:P, 1:LEN - 2], ALU.add))
                    nc.gpsimd.tensor_copy(win4[0:64, SP:LEN], win2[0:64, SP:LEN]).then_inc(win_done, 1)
                else:
                    pstep(nc.gpsimd.tensor_tensor(win8[:, 3:LEN], win2[:, 3:LEN], win2[:, 1:LEN - 2], ALU.add))
                    pstep(nc.gpsimd.tensor_tensor(win2[:, 7:LEN], win8[:, 7:LEN], win8[:, 3:LEN - 4], ALU.add))
                    pstep(nc.gpsimd.tensor_tensor(win4[64:P, SP:LEN], win2[64:P, SP:LEN], win2[64:P, SP - 8:LEN - 8],
                                                  ALU.add))
                    nc.gpsimd.tensor_copy(win4[0:64, SP:LEN], win2[0:64, SP:LEN]).then_inc(win_done, 1)
            for buf, first, chunks, start, hist in ((ua, 0, CA, WA, SA), (ub, CA, CB, WB, SB), (pc, CA + CB, CC, WP, SP)):
                nc.gpsimd.tensor_copy(steps[:, first:first + chunks, :].rearrange("p m (b l) -> p m b l", b=NSEQ),
                                      buf[:, :, start:].rearrange("p m (b l) -> p m b l", b=NSEQ)[:, :, :, hist:]
                                      ).then_inc(steps_ready, 1)
            pool.wait_ge(act_read, J.read("new_p_sample"))
            pool.dma_start(na_p[0, 0], new_rows[0:SA, 0, :]).then_inc(state_out, 16)
            pool.dma_start(nb_p[0, 0], new_rows[0:SB, 2, :]).then_inc(state_out, 16)
            pool.dma_start(np_p[0, 0], new_rows[0:SP, 4, 0:DC]).then_inc(state_out, 16)
            for b in range(NSEQ):
                r = STEPS * b
                pool.dma_start(na_s[0, b], new_rows[r + STEPS - SA:r + STEPS, 1, :]).then_inc(state_out, 16)
                pool.dma_start(nb_s[0, b, SB - STEPS:SB, :], new_rows[r:r + STEPS, 3, :]).then_inc(state_out, 16)
                pool.dma_start(np_s[0, b, SP - STEPS:SP, :], new_rows[r:r + STEPS, 5, 0:DC]).then_inc(state_out, 16)
            pool.wait_ge(psum_full, J.full(f"out{C - 1}"))
            for c in range(C):
                nc.gpsimd.memset(acc[:, c, :], 0.0).then_inc(acc_added, 1)
            nc.gpsimd.memset(gate_row[:, 0, :], 1.0 / E).then_inc(shared_gate, 1)

            def d_low_item(n, slot):
                pool.wait_ge(hi_done["d"], n + 1)
                nc.gpsimd.tensor_tensor(d_lo[:, :, :], d_raw[:, slot, :, :], d_hi[:, :, :].bitcast(F32),
                                        ALU.subtract).then_inc(lo_done["d"], 1)

            d_low_item(0, 0)
            with pool.Fori(0, E // 2) as i:
                d_low_item(i * 2 + 1, 1)
                d_low_item(i * 2 + 2, 0)

        def rsqrt_root(act, i):
            act.wait_ge(dve_read, J.read(f"rms{i + 1}"))
            nc.scalar.activation(rstd[:, :], rstd[:, :], ACT.Sqrt).then_inc(root[i], 1)

        def modulate_prompt(act, i, shift):
            act.wait_ge(xn_ready[i], 1)
            for c in range(C):
                nc.scalar.activation(hT[:, c, 0:SEQ], hT[:, c, 0:SEQ], ACT.Identity, bias=mod[:, shift, c, 0:1],
                                     scale=gmul[:, c, 0:1]).then_inc(h_prompt[i], 1)

        def high(kind, n, slot):
            hi, _, raw = GUCOL[kind]
            nc.scalar.wait_ge(raw_in[kind, slot], raw_count(n, slot))
            if not (isinstance(n, int) and n < 2):
                nc.scalar.wait_ge(gu_done, n - 1)
            nc.scalar.activation(hi[:, slot, :, :], raw[:, slot, :, :], ACT.Copy).then_inc(hi_done[kind], 1)

        def raw_count(n, slot):
            return (n - slot) * 8 + 16

        def down_high(n, slot):
            nc.scalar.wait_ge(raw_in["d", slot], raw_count(n, slot))
            if not (isinstance(n, int) and n == 0):
                nc.scalar.wait_ge(down_full, n * C)
            nc.scalar.activation(d_hi[:, :, :], d_raw[:, slot, :, :], ACT.Copy).then_inc(hi_done["d"], 1)

        def act_item(n, slot, next_item, down_of):
            if down_of is not None:
                down_high(down_of, 1 - slot)
            if next_item is not None:
                high("g", next_item, 1 - slot)
                high("u", next_item, 1 - slot)
            nc.scalar.wait_ge(gu_done, n + 1)
            if not (isinstance(n, int) and n == 0):
                nc.scalar.wait_ge(up_done, n)
            nc.scalar.activation(sil[:, :, :], gu_ps[:, 0:FC, 0:T], ACT.Silu).then_inc(silu_done, 1)
            nc.scalar.wait_ge(hid_done, n + 1)
            if not (isinstance(n, int) and n == 0):
                nc.scalar.wait_ge(down_full, n * C)
            nc.scalar.activation(hid_hi[:, :, :], hid[:, :, :], ACT.Copy).then_inc(hid_hi_done, 1)

        @block.scalar
        def _(act):
            act.dma_start(rows[0:KB, :], conv_b_w[0]).then_inc(rows_in, 16)
            act.dma_start(rows[KB:KB + KA, :], conv_a_w[0]).then_inc(rows_in, 16)
            for i, v in enumerate((conv_b_bias, ln_b_g, ln_b_b)):
                act.dma_start(rows[KB + KA + i:KB + KA + i + 1, :], v).then_inc(rows_in, 16)
            act.dma_start(rows[37:38, 0:DC], pool_scale).then_inc(rows_in, 16)
            act.dma_start(rows[37:38, DC:DA], pool_scale[:, 0:DA - DC]).then_inc(rows_in, 16)
            act.dma_start(hist_a[:, :], state_a[0].rearrange("b t d -> (b t) d")).then_inc(hist_in, 16)
            sb_v = state_b[0].rearrange("(h b) t d -> h (b t) d", h=2)
            for h in range(2):
                act.dma_start(hist_b[:, h, :], sb_v[h]).then_inc(hist_in, 16)
            act.dma_start(hist_p[:, :], state_p[0].rearrange("b t d -> (b t) d")).then_inc(hist_in, 16)
            act.wait_ge(c_in, 32)
            nc.scalar.activation(c_sil[:, :], c_tok[:, :], ACT.Silu).then_inc(c_silu, 1)

            def ready(name):
                act.wait_ge(psum_full, J.full(name))
                return tile(name)

            for c in range(C):
                nc.scalar.activation(xT[:, c, :], ready(f"x{c}")[:, 0:T], ACT.Copy).then_inc(act_read, 1)
            rsqrt_root(act, 0)
            modulate_prompt(act, 0, 0)
            for m in range(CB):
                ps = ready(f"gb{m}")
                if m:
                    act.wait_ge(dve_read, J.read(f"ab{m - 1}"))
                nc.scalar.activation(sig[:, :], ps[:, 0:T], ACT.Sigmoid).then_inc(act_read, 1)
            for m in range(CA):
                nc.scalar.activation(cat[:, CA + m, :], ready(f"xa{m}")[:, 0:T], ACT.Copy).then_inc(act_read, 1)
                ps = ready(f"ca{m}")
                nc.scalar.activation(ua[:, m, SA:WA], ps[:, 0:SEQ], ACT.Copy)
                nc.scalar.activation(ua[:, m, WA:].rearrange("p (b l) -> p b l", b=NSEQ)[:, :, SA:],
                                     ps[:, SEQ:T].rearrange("p (b l) -> p b l", b=NSEQ), ACT.Copy).then_inc(act_read, 1)
                nc.scalar.activation(ba[:, m, :], ready(f"ba{m}")[:, 0:T], ACT.Copy).then_inc(act_read, 1)
            for m in range(CC):
                ps = ready(f"pc{m}")
                nc.scalar.activation(pc[:, m, SP:WP], ps[:, 0:SEQ], ACT.Copy)
                nc.scalar.activation(pc[:, m, WP:].rearrange("p (b l) -> p b l", b=NSEQ)[:, :, SP:],
                                     ps[:, SEQ:T].rearrange("p (b l) -> p b l", b=NSEQ), ACT.Copy).then_inc(act_read, 1)
            for i, (name, rows_n, cols) in enumerate((("new_a_prompt", SA, DA), ("new_a_sample", NS, DA),
                                                      ("new_b_prompt", SB, DB), ("new_b_sample", NS, DB),
                                                      ("new_p_prompt", SP, DC), ("new_p_sample", NS, DC))):
                nc.scalar.activation(new_rows[0:rows_n, i, 0:cols], ready(name)[0:rows_n, 0:cols],
                                     ACT.Copy).then_inc(act_read, 1)
            act.wait_ge(dve_read, J.read("ln_var"))
            nc.scalar.activation(rstd[:, :], rstd[:, :], ACT.Sqrt).then_inc(ln_rt, 1)
            act.wait_ge(lnn, 1)
            act.wait_ge(ua_done, 2 * CA)
            for m in range(CB):
                nc.scalar.activation(cat[:, CA + m, :], vb[:, m, :], ACT.Silu, bias=vecs[:, m, 36:37],
                                     scale=vecs[:, m, 35:36]).then_inc(cat_b, 1)
            high("g", 0, 0)
            high("u", 0, 0)
            rsqrt_root(act, 1)
            modulate_prompt(act, 1, 3)
            act.wait_ge(h_sample[1], 1)
            act.wait_ge(h_prompt[1], C)
            act.wait_ge(psum_full, J.full("rms2"))
            nc.scalar.activation(h_hi[:, :, :], hT[:, :, :], ACT.Copy).then_inc(h_hi_ready, 1)
            ps = ready("router")
            nc.scalar.activation(score[:, :, :], ps[0:TT, 0:NT * E].rearrange("p (a e) -> p a e", a=NT),
                                 ACT.Sigmoid).then_inc(act_read, 1)
            act_item(0, 0, next_item=1, down_of=None)
            with act.Fori(0, (E - 2) // 2) as i:
                act_item(i * 2 + 1, 1, next_item=i * 2 + 2, down_of=i * 2)
                act_item(i * 2 + 2, 0, next_item=i * 2 + 3, down_of=i * 2 + 1)
            act_item(E - 1, 1, next_item=E, down_of=E - 2)
            act_item(E, 0, next_item=None, down_of=E - 1)
            down_high(E, 0)
            act.wait_ge(x2_mean, 1)
            nc.scalar.activation(rstd[:, :], rstd[:, :], ACT.Sqrt).then_inc(root[2], 1)
            for k in range(2 * NT):
                act.wait_ge(y_full, k + 1)
                nc.scalar.activation(y_tok[:, k // 2, (k % 2) * 512:(k % 2) * 512 + 512], bank[1 + k][0:TT, :],
                                     ACT.Copy).then_inc(y_copied, 1)

        def low(kind, n, slot):
            hi, lo, raw = GUCOL[kind]
            nc.vector.wait_ge(hi_done[kind], n + 1)
            nc.vector.tensor_tensor(lo[:, slot, :, :], raw[:, slot, :, :], hi[:, slot, :, :].bitcast(F32),
                                    ALU.subtract).then_inc(lo_done[kind], 1)

        def add_down(count):
            nc.vector.wait_ge(acc_added, count * C)
            for c in range(C):
                nc.vector.wait_ge(down_full, (count - 1) * C + c + 1)
                nc.vector.tensor_tensor(acc[:, c, :], bank[5 + c % 3][:, 0:T], acc[:, c, :], ALU.add)\
                    .then_inc(acc_added, 1)

        def dve_item(n, slot, next_item):
            zero = isinstance(n, int) and n == 0
            if not zero:
                nc.vector.wait_ge(gate_bc_done, n)
                nc.vector.tensor_scalar(gate_row[:, slot, :], gatesT[:, :], ident[0:E, bass.ds(n - 1, 1)], None,
                                        ALU.mult).then_inc(gate_row_done, 1)
            if next_item is not None:
                low("g", next_item, 1 - slot)
                low("u", next_item, 1 - slot)
            nc.vector.wait_ge(silu_done, n + 1)
            if not zero:
                nc.vector.wait_ge(hid_done, n)
            nc.vector.tensor_tensor(prod[:, :, :], sil[:, :, :], gu_ps[:, FC:2 * FC, 0:T], ALU.mult)\
                .then_inc(up_done, 1)
            nc.vector.wait_ge(up_done, n + 1)
            nc.vector.wait_ge(gate_bc_done, n + 1)
            if not zero:
                nc.vector.wait_ge(hid_lo_done, n)
            nc.vector.tensor_tensor(hid[:, :, :], prod[:, :, :], bank[4][:, 0:T].unsqueeze(1)
                                    .broadcast_to([P, FC, T]), ALU.mult).then_inc(hid_done, 1)
            if not zero:
                add_down(n)
            nc.vector.wait_ge(hid_hi_done, n + 1)
            nc.vector.tensor_tensor(hid_lo[:, :, :], hid[:, :, :], hid_hi[:, :, :].bitcast(F32), ALU.subtract)\
                .then_inc(hid_lo_done, 1)

        @block.vector
        def _(dve):
            steps = [0]

            def chain(ins):
                steps[0] += 1
                ins.then_inc(vstep, 1)
                dve.wait_ge(vstep, steps[0])

            def ready(name):
                dve.wait_ge(psum_full, J.full(name))
                return tile(name)

            def seqs(ap):
                return ap.rearrange("p (b l) -> p b l", b=NSEQ)

            dve.wait_ge(pads, 4)
            for j in range(CC):
                for h in range(2):
                    chain(nc.vector.tensor_scalar(invc[64 * h:64 * h + 64, j, :], iota_i[64 * h:64 * h + 64, :],
                                                  float(WINDOWS[2 * j + h]), None, ALU.min))
            chain(nc.vector.reciprocal(invc[:, :, :], invc[:, :, :]))
            nc.vector.tensor_copy(cT[:, :, :], ready("cT")[:, 0:C * N_SEQ_ALL].rearrange("p (c s) -> p c s", c=C)
                                  ).then_inc(dve_read, 1)
            nc.vector.tensor_copy(vecs[:, :, :], ready("vec")[:, 0:3 * 38].rearrange("p (a b) -> p a b", a=3)
                                  ).then_inc(dve_read, 1)
            def put_hist(name, buf, chunks, start, length, rows_n, b0, nb):
                ps = ready(name)[:, 0:chunks * nb * rows_n].rearrange("p (m b r) -> p m b r", m=chunks, b=nb)
                dst = buf[:, :, start + b0 * length:start + (b0 + nb) * length]
                nc.vector.tensor_copy(dst.rearrange("p m (b l) -> p m b l", b=nb)[:, :, :, 0:rows_n], ps)\
                    .then_inc(dve_read, 1)

            put_hist("hist_a", ua, CA, WA, LA, SA, 0, NSEQ)
            put_hist("hist_b0", ub, CB, WB, LB, SB, 0, 4)
            put_hist("hist_b1", ub, CB, WB, LB, SB, 4, 4)
            put_hist("hist_p", pc, CC, WP, LP, SP, 0, NSEQ)
            dve.wait_ge(bada_in, 16)
            dve.wait_ge(smallv_in, 48)

            def take_mod(g):
                nc.vector.tensor_tensor(mod[:, g, :, :],
                                        ready(f"mod{g}")[:, 0:C * N_SEQ_ALL].rearrange("p (c s) -> p c s", c=C),
                                        badaT[:, g, :].unsqueeze(2).broadcast_to([P, C, N_SEQ_ALL]),
                                        ALU.add).then_inc(dve_read, 1)
                dve.wait_ge(dve_read, J.read(f"mod{g}"))

            def norm_factor(i, scale_group):
                chain(nc.vector.tensor_scalar(gmul[:, :, :], mod[:, scale_group, :, :], 1.0, None, ALU.add))
                chain(nc.vector.tensor_tensor(gmul[:, :, :], gmul[:, :, :],
                                              smallv[:, i, :].unsqueeze(2).broadcast_to([P, C, N_SEQ_ALL]), ALU.mult))

            def mean_square(ps, count, reads):
                nc.vector.tensor_scalar(rstd[:, :], ps[:, 0:T], 1.0 / count, EPS, ALU.mult, ALU.add).then_inc(reads, 1)

            def by_token(ap, n):
                return ap.unsqueeze(1).broadcast_to([P, n, T])

            def sample(ap):
                return ap[:, :, SEQ:T].rearrange("p c (b l) -> p c b l", b=NSEQ)

            def rms(i, name, shift):
                mean_square(ready(name), D, dve_read)
                dve.wait_ge(root[i], 1)
                chain(nc.vector.reciprocal(rstd[:, :], rstd[:, :]))
                nc.vector.tensor_tensor(hT[:, :, :], xT[:, :, :], by_token(rstd[:, :], C), ALU.mult)\
                    .then_inc(xn_ready[i], 1)
                dve.wait_ge(xn_ready[i], 1)
                chain(nc.vector.tensor_tensor(sample(hT), sample(hT), gmul[:, :, 1:].unsqueeze(3)
                                              .broadcast_to([P, C, NSEQ, STEPS]), ALU.mult))
                nc.vector.tensor_tensor(sample(hT), sample(hT), mod[:, shift, :, 1:].unsqueeze(3)
                                        .broadcast_to([P, C, NSEQ, STEPS]), ALU.add).then_inc(h_sample[i], 1)

            dve.wait_ge(act_read, J.read(f"x{C - 1}"))
            nc.vector.tensor_tensor(sq1[:, :, :], xT[:, :, :], xT[:, :, :], ALU.mult).then_inc(sq_ready[0], 1)
            take_mod(1)
            take_mod(0)
            norm_factor(0, 1)
            rms(0, "rms1", 0)
            for m in range(CB):
                ps = ready(f"ab{m}")
                dve.wait_ge(act_read, J.read(f"gb{m}"))
                nc.vector.tensor_tensor(ub[:, m, SB:WB], ps[:, 0:SEQ], sig[:, 0:SEQ], ALU.mult).then_inc(ub_ready, 1)
                nc.vector.tensor_tensor(ub[:, m, WB:].rearrange("p (b l) -> p b l", b=NSEQ)[:, :, SB:], seqs(ps[:, SEQ:T]),
                                        seqs(sig[:, SEQ:T]), ALU.mult).then_inc(dve_read, 1)

            def conv(dst, buf, m, start, length, taps, tap0, bias):
                views = [(dst[:, m, 0:SEQ], lambda k: buf[:, m, k:k + SEQ]),
                         (seqs(dst[:, m, SEQ:T]), lambda k: buf[:, m, start:].rearrange("p (b l) -> p b l", b=NSEQ)
                          [:, :, k:k + STEPS])]
                for k in range(taps):
                    w = vecs[:, m, tap0 + k:tap0 + k + 1]
                    for out, src in views:
                        if k:
                            dve.wait_ge(vstep, steps[0] - 1)
                            ins = nc.vector.scalar_tensor_tensor(out, src(k), w, out, ALU.mult, ALU.add)
                        elif bias is not None:
                            ins = nc.vector.tensor_scalar(out, src(0), w, bias, ALU.mult, ALU.add)
                        else:
                            ins = nc.vector.tensor_scalar(out, src(0), w, None, ALU.mult)
                        steps[0] += 1
                        ins.then_inc(vstep, 1)
                dve.wait_ge(vstep, steps[0])

            dve.wait_ge(dve_read, J.read(f"ab{CB - 1}"))
            dve.wait_ge(ub_ready, CB)
            conv(vb, ub, 0, WB, LB, KB, 0, vecs[:, 0, 34:35])
            take_mod(2)
            conv(vb, ub, 1, WB, LB, KB, 0, vecs[:, 1, 34:35])
            take_mod(3)
            conv(vb, ub, 2, WB, LB, KB, 0, vecs[:, 2, 34:35])
            take_mod(4)
            take_mod(5)
            for m in range(CA):
                dve.wait_ge(ua_done, 2 * m + 2)
                conv(va, ua, m, WA, LA, KA, KB, None)
            dve.wait_ge(act_read, J.read(f"ba{CA - 1}"))
            nc.vector.tensor_tensor(cat[:, 0:CA, :], va[:, :, :], ba[:, :, :], ALU.mult).then_inc(cat_a, 1)
            for m in range(CC):
                dve.wait_ge(win_done, m + 1)
                inv = invc[:, m, KP - 1:KP]
                chain(nc.vector.scalar_tensor_tensor(diff[:, m, 0:SEQ], win4[:, SP:WP], inv, pc[:, m, SP:WP],
                                                     ALU.mult, ALU.subtract))
                chain(nc.vector.scalar_tensor_tensor(
                    seqs(diff[:, m, SEQ:T]), win4[:, WP:].rearrange("p (b l) -> p b l", b=NSEQ)[:, :, SP:], inv,
                    pc[:, m, WP:].rearrange("p (b l) -> p b l", b=NSEQ)[:, :, SP:], ALU.mult, ALU.subtract))
                chain(nc.vector.tensor_tensor(diff[:, m, 0:KP], win4[:, SP:SP + KP], invc[:, m, :], ALU.mult))
                nc.vector.tensor_tensor(diff[:, m, 0:KP], diff[:, m, 0:KP], pc[:, m, SP:SP + KP], ALU.subtract)\
                    .then_inc(diff_ready, 1)
            for m in range(CC):
                nc.vector.tensor_scalar(cat[:, CA + CB + m, :], ready(f"pool{m}")[:, 0:T], vecs[:, m, 37:38], None,
                                        ALU.mult).then_inc(dve_read, 1)
            nc.vector.tensor_scalar(rstd[:, :], ready("ln_sum")[:, 0:T], 1.0 / DB, None, ALU.mult).then_inc(dve_read, 1)
            dve.wait_ge(dve_read, J.read("ln_sum"))
            chain(nc.vector.tensor_tensor(vb[:, :, :], vb[:, :, :], by_token(rstd[:, :], CB), ALU.subtract))
            dve.wait_ge(psum_full, J.full("new_b_sample"))
            nc.vector.tensor_tensor(ln_sq_t[:, :, :], vb[:, :, :], vb[:, :, :], ALU.mult).then_inc(ln_sq_ready, 1)
            mean_square(ready("ln_var"), DB, dve_read)
            dve.wait_ge(ln_rt, 1)
            chain(nc.vector.reciprocal(rstd[:, :], rstd[:, :]))
            nc.vector.tensor_tensor(vb[:, :, :], vb[:, :, :], by_token(rstd[:, :], CB), ALU.mult).then_inc(lnn, 1)
            low("g", 0, 0)
            low("u", 0, 0)
            for c in range(C):
                ps = ready(f"out{c}")
                nc.vector.scalar_tensor_tensor(xT[:, c, 0:SEQ], ps[:, 0:SEQ], mod[:, 2, c, 0:1], xT[:, c, 0:SEQ],
                                               ALU.mult, ALU.add)
                nc.vector.tensor_tensor(tmps[:, c, :, :], seqs(ps[:, SEQ:T]),
                                        mod[:, 2, c, 1:].unsqueeze(2).broadcast_to([P, NSEQ, STEPS]),
                                        ALU.mult).then_inc(dve_read, 1)
            dve.wait_ge(dve_read, J.read(f"out{C - 1}"))
            chain(nc.vector.tensor_tensor(sample(xT), sample(xT), tmps[:, :, :, :], ALU.add))
            nc.vector.tensor_tensor(sq2[:, :, :], xT[:, :, :], xT[:, :, :], ALU.mult).then_inc(sq_ready[1], 1)
            norm_factor(1, 4)
            dve.wait_ge(state_out, 16 * (5 + 3 * NSEQ))
            rms(1, "rms2", 3)
            dve.wait_ge(h_hi_ready, 1)
            nc.vector.tensor_tensor(h_lo[:, :, :], hT[:, :, :], h_hi[:, :, :].bitcast(F32), ALU.subtract)\
                .then_inc(h_lo_ready, 1)
            dve.wait_ge(router_in, 32)
            dve.wait_ge(lowmask, 2)
            dve.wait_ge(act_read, J.read("router"))
            G = NT * GROUPS
            grouped = biased[:, :, :].rearrange("p a (g k) -> p (a g) k", g=GROUPS)

            def each(ap, k=GROUPS):
                return ap.unsqueeze(2).broadcast_to([TT, G, k])

            chain(nc.vector.tensor_tensor(biased[:, :, :], score[:, :, :],
                                          bias_rt[:, :].unsqueeze(1).broadcast_to([TT, NT, E]), ALU.add))
            chain(nc.vector.tensor_reduce(gs[:, 0, :], grouped, AX_X, ALU.max))
            chain(nc.vector.tensor_tensor(pair[:, :, :], grouped, each(gs[:, 0, :]), ALU.is_equal))
            chain(nc.vector.tensor_reduce(gs[:, 1, :], pair[:, :, :], AX_X, ALU.add))
            chain(nc.vector.scalar_tensor_tensor(pair2[:, :, :], pair[:, :, :], -BIG, grouped, ALU.mult, ALU.add))
            chain(nc.vector.tensor_reduce(gs[:, 2, :], pair2[:, :, :], AX_X, ALU.max))
            chain(nc.vector.tensor_scalar(gs[:, 1, :], gs[:, 1, :], 2.0, -BIG, ALU.is_lt, ALU.mult))
            chain(nc.vector.tensor_tensor(gs[:, 1, :], gs[:, 1, :], gs[:, 0, :], ALU.add))
            chain(nc.vector.tensor_tensor(gs[:, 2, :], gs[:, 2, :], gs[:, 1, :], ALU.max))
            chain(nc.vector.tensor_tensor(gs[:, 3, :], gs[:, 0, :], gs[:, 2, :], ALU.add))
            s4 = gs[:, 3, :].rearrange("p (a g) -> p a g", a=NT)
            other = s4.unsqueeze(2).broadcast_to([TT, NT, GROUPS, GROUPS])
            own = s4.unsqueeze(3).broadcast_to([TT, NT, GROUPS, GROUPS])
            p4 = pair[:, :, :].rearrange("p (a g) k -> p a g k", a=NT)
            q4 = pair2[:, :, :].rearrange("p (a g) k -> p a g k", a=NT)
            chain(nc.vector.tensor_tensor(p4, other, own, ALU.is_gt))
            chain(nc.vector.tensor_tensor(q4, other, own, ALU.is_equal))
            chain(nc.vector.tensor_tensor(q4, q4, lower[:, :, :].unsqueeze(1).broadcast_to([TT, NT, GROUPS, GROUPS]),
                                          ALU.mult))
            chain(nc.vector.tensor_tensor(pair[:, :, :], pair[:, :, :], pair2[:, :, :], ALU.add))
            chain(nc.vector.tensor_reduce(gs[:, 0, :], pair[:, :, :], AX_X, ALU.add))
            chain(nc.vector.tensor_scalar(gs[:, 0, :], gs[:, 0, :], float(TOPG), None, ALU.is_lt))
            ra = rt_a[:, :, :].rearrange("p a (g k) -> p (a g) k", g=GROUPS)
            chain(nc.vector.tensor_tensor(ra, grouped, each(gs[:, 0, :]), ALU.mult))
            chain(nc.vector.tensor_scalar(gs[:, 1, :], gs[:, 0, :], BIG, -BIG, ALU.mult, ALU.add))
            chain(nc.vector.tensor_tensor(ra, ra, each(gs[:, 1, :]), ALU.add))
            for a in range(NT):
                chain(nc.vector.max(top8[:, a, :], rt_a[:, a, :]))
                chain(nc.vector.match_replace(rt_b[:, a, :], top8[:, a, :], rt_a[:, a, :], -3e38))
            chain(nc.vector.tensor_tensor(rt_b[:, :, :], rt_b[:, :, :], rt_a[:, :, :], ALU.not_equal))
            chain(nc.vector.tensor_tensor(rt_b[:, :, :], rt_b[:, :, :], score[:, :, :], ALU.mult))
            chain(nc.vector.tensor_reduce(gsum[:, 0, :], rt_b[:, :, :], AX_X, ALU.add))
            chain(nc.vector.reciprocal(gsum[:, 1, :], gsum[:, 0, :]))
            nc.vector.scalar_tensor_tensor(gates[:, :, :], rt_b[:, :, :], SCALE,
                                           gsum[:, 1, :].unsqueeze(2).broadcast_to([TT, NT, E]), ALU.mult,
                                           ALU.mult).then_inc(gates_ready, 1)
            nc.vector.tensor_copy(gatesT[:, :], ready("gatesT")[0:E, 0:T]).then_inc(dve_read, 1)
            dve.wait_ge(dve_read, J.read("gatesT"))
            dve_item(0, 0, next_item=1)
            with dve.Fori(0, (E - 2) // 2) as i:
                dve_item(i * 2 + 1, 1, next_item=i * 2 + 2)
                dve_item(i * 2 + 2, 0, next_item=i * 2 + 3)
            dve_item(E - 1, 1, next_item=E)
            dve_item(E, 0, next_item=None)
            add_down(E + 1)
            dve.wait_ge(acc_added, C * (E + 2))
            for c in range(C):
                nc.vector.scalar_tensor_tensor(xT[:, c, 0:SEQ], acc[:, c, 0:SEQ], mod[:, 5, c, 0:1], xT[:, c, 0:SEQ],
                                               ALU.mult, ALU.add)
            chain(nc.vector.tensor_tensor(tmps[:, :, :, :], sample(acc), mod[:, 5, :, 1:].unsqueeze(3)
                                          .broadcast_to([P, C, NSEQ, STEPS]), ALU.mult))
            chain(nc.vector.tensor_tensor(sample(xT), sample(xT), tmps[:, :, :, :], ALU.add))
            nc.vector.tensor_tensor(sqT[:, :, :], xT[:, :, :], xT[:, :, :], ALU.mult).then_inc(sq_ready[2], 1)
            dve.wait_ge(x2_square, 1)
            mean_square(bank[0], D, x2_mean)
            dve.wait_ge(root[2], 1)
            chain(nc.vector.reciprocal(rstd[:, :], rstd[:, :]))
            for c in range(C):
                nc.vector.scalar_tensor_tensor(yT[:, c, :], xT[:, c, :], smallv[:, 2, c:c + 1], rstd[:, :],
                                               ALU.mult, ALU.mult).then_inc(yn_ready, 1)

        @block.tensor
        def _(pe):
            def start(name):
                last = J.before(name)
                if last is not None:
                    pe.wait_ge(act_read if J.reader[last] == "act" else dve_read, J.read(last))
                return tile(name)

            def done(ins):
                ins.then_inc(psum_full, 1)

            def transposes(name, parts):
                ps = start(name)
                at_col = 0
                for src, n_rows, n_cols in parts:
                    ins = nc.tensor.transpose(ps[0:n_cols, at_col:at_col + n_rows], src, ident[0:n_rows, 0:n_rows])
                    at_col += n_rows
                done(ins)

            def sum_product(name, pairs, cols=T):
                ps = start(name)
                for i, (a, b) in enumerate(pairs):
                    ins = nc.tensor.matmul(ps[:, 0:cols], a, b, start=(i == 0), stop=(i == len(pairs) - 1))
                done(ins)

            pe.wait_ge(consts, 2)
            pe.wait_ge(c_silu, 1)
            transposes("cT", [(c_sil[:, c * P:(c + 1) * P], N_SEQ_ALL, P) for c in range(C)])
            pe.wait_ge(x_in, 64)
            for c in range(C):
                transposes(f"x{c}", [(x_tok[:, a, c * P:(c + 1) * P], TT, P) for a in range(NT)])
            pe.wait_ge(rows_in, 112)
            transposes("vec", [(rows[:, m * P:(m + 1) * P], 38, P) for m in range(3)])
            pe.wait_ge(hist_in, 64)
            transposes("hist_a", [(hist_a[:, m * P:(m + 1) * P], NSEQ * SA, P) for m in range(CA)])
            for h in range(2):
                transposes(f"hist_b{h}", [(hist_b[:, h, m * P:(m + 1) * P], 4 * SB, P) for m in range(CB)])
            transposes("hist_p", [(hist_p[:, m * P:(m + 1) * P], NSEQ * SP, P) for m in range(CC)])

            def modulation(order, g):
                slot, nth = order % 2, {1: 1, 0: 1, 2: 2, 3: 2, 4: 3, 5: 3}[g]
                pe.wait_ge(ada_in[slot], 16 * nth)
                ps = start(f"mod{g}")
                for n in range(C):
                    for k in range(C):
                        ins = nc.tensor.matmul(ps[:, n * N_SEQ_ALL:(n + 1) * N_SEQ_ALL],
                                               ada[slot][:, k, n * P:(n + 1) * P], cT[:, k, :],
                                               start=(k == 0), stop=(k == C - 1))
                done(ins)

            pe.wait_ge(dve_read, J.read("cT"))
            modulation(1, 1)
            modulation(0, 0)
            pe.wait_ge(sq_ready[0], 1)
            sum_product("rms1", [(ones[:, :], sq1[:, c, :]) for c in range(C)])

            def project(name, col):
                sum_product(name, [(w_in_sb[:, k, col:col + P], hT[:, k, :]) for k in range(C)])

            pe.wait_ge(h_prompt[0], C)
            pe.wait_ge(h_sample[0], 1)
            pe.wait_ge(win_in[0], 16)
            for m in range(CB):
                project(f"gb{m}", 3 * DA + DB + m * P)
                project(f"ab{m}", 3 * DA + m * P)
            modulation(1, 2)
            pe.wait_ge(win_in[1], 16)
            for m in range(CA):
                project(f"xa{m}", m * P)
                project(f"ca{m}", DA + m * P)
                project(f"ba{m}", 2 * DA + m * P)
            modulation(0, 3)
            pe.wait_ge(win_in[2], 16)
            for m in range(CC):
                project(f"pc{m}", 3 * DA + 2 * DB + m * P)
            modulation(1, 4)
            modulation(0, 5)

            def new_rows_of(key, buf, chunks, first, start_col, hist):
                for kind, n_rows in (("prompt", hist), ("sample", NS)):
                    ps = start(f"new_{key}_{kind}")
                    for m in range(chunks):
                        src = buf[:, m, start_col - hist:start_col] if kind == "prompt" else steps[:, first + m, :]
                        ins = nc.tensor.transpose(ps[0:n_rows, m * P:(m + 1) * P], src, ident[:, :])
                    done(ins)

            pe.wait_ge(steps_ready, 3)
            new_rows_of("a", ua, CA, 0, WA, SA)
            new_rows_of("b", ub, CB, CA, WB, SB)
            new_rows_of("p", pc, CC, CA + CB, WP, SP)
            pe.wait_ge(pw_in, 64)
            pe.wait_ge(diff_ready, CC)
            for m in range(CC):
                sum_product(f"pool{m}", [(pw[:, m, :], diff[:, m, :])])
            pe.wait_ge(dve_read, J.read("mod4"))
            sum_product("ln_sum", [(ones[:, :], vb[:, m, :]) for m in range(CB)])
            pe.wait_ge(ln_sq_ready, 1)
            sum_product("ln_var", [(ones[:, :], ln_sq_t[:, m, :]) for m in range(CB)])
            pe.wait_ge(wout_in, 16)
            pe.wait_ge(cat_a, 1)
            pe.wait_ge(cat_b, CB)
            pe.wait_ge(dve_read, J.read(f"pool{CC - 1}"))
            for c in range(C):
                sum_product(f"out{c}", [(w_out_sb[:, k, c * P:(c + 1) * P], cat[:, k, :]) for k in range(C)])
            pe.wait_ge(sq_ready[1], 1)
            sum_product("rms2", [(ones[:, :], sq2[:, c, :]) for c in range(C)])
            pe.wait_ge(h_prompt[1], C)
            pe.wait_ge(h_sample[1], 1)
            pe.wait_ge(router_in, 32)
            ps = start("router")
            for a in range(NT):
                for k in range(C):
                    ins = nc.tensor.matmul(ps[0:TT, a * E:(a + 1) * E], hT[:, k, a * TT:(a + 1) * TT], w_rt[:, k, :],
                                           start=(k == 0), stop=(k == C - 1))
            done(ins)

            def exact(ps, terms):
                passes = [(a, b) for (ah, al), (bh, bl) in terms for a, b in ((al, bh), (ah, bl), (ah, bh))]
                for i, (a, b) in enumerate(passes):
                    ins = nc.tensor.matmul(ps, a, b, start=(i == 0), stop=(i == len(passes) - 1))
                return ins

            def gate_up(n, slot):
                zero = isinstance(n, int) and n == 0
                for j, kind in enumerate("gu"):
                    pe.wait_ge(lo_done[kind], n + 1)
                    if not zero:
                        pe.wait_ge(silu_done if kind == "g" else up_done, n)
                    hi, lo, _ = GUCOL[kind]
                    for f in range(FC):
                        cols = slice(f * P, (f + 1) * P)
                        ins = exact(gu_ps[:, FC * j + f, 0:T],
                                    [((hi[:, slot, k, cols], lo[:, slot, k, cols]), (h_hi[:, k, :], h_lo[:, k, :]))
                                     for k in range(C)])
                ins.then_inc(gu_done, 1)

            def gate_broadcast(n, slot):
                if not (isinstance(n, int) and n == 0):
                    pe.wait_ge(gate_row_done, n)
                    pe.wait_ge(hid_done, n)
                nc.tensor.matmul(bank[4][:, 0:T], ones[0:E, :], gate_row[:, slot, :], start=True, stop=True)\
                    .then_inc(gate_bc_done, 1)

            def down(n, zero=False):
                pe.wait_ge(hid_lo_done, n + 1)
                pe.wait_ge(lo_done["d"], n + 1)
                for c in range(C):
                    cols = slice(c * P, (c + 1) * P)
                    if c >= 3:
                        pe.wait_ge(acc_added, n * C + C + c - 2)
                    elif not zero:
                        pe.wait_ge(acc_added, n * C + {0: 7, 1: 8, 2: 6}[c])
                    exact(bank[5 + c % 3][:, 0:T],
                          [((d_hi[:, f, cols], d_lo[:, f, cols]), (hid_hi[:, f, :], hid_lo[:, f, :]))
                           for f in range(FC)]).then_inc(down_full, 1)

            pe.wait_ge(h_hi_ready, 1)
            pe.wait_ge(h_lo_ready, 1)
            pe.wait_ge(act_read, J.read("router"))
            gate_up(0, 0)
            pe.wait_ge(gates_ready, 1)
            ps = start("gatesT")
            for a in range(NT):
                ins = nc.tensor.transpose(ps[0:E, a * TT:(a + 1) * TT], gates[:, a, :], ident[0:TT, 0:TT])
            done(ins)
            pe.wait_ge(dve_read, J.read("gatesT"))
            pe.wait_ge(shared_gate, 1)
            gate_broadcast(0, 0)
            gate_up(1, 1)
            gate_broadcast(1, 1)
            down(0, zero=True)
            gate_up(2, 0)
            gate_broadcast(2, 0)
            down(1)
            with pe.Fori(1, E // 2) as i:
                for s in range(2):
                    n = i * 2 + 1 + s
                    gate_up(n, 1 - s)
                    gate_broadcast(n, 1 - s)
                    down(n - 1)
            down(E)
            pe.wait_ge(sq_ready[2], 1)
            for c in range(C):
                ins = nc.tensor.matmul(bank[0][:, 0:T], ones[:, :], sqT[:, c, :], start=(c == 0), stop=(c == C - 1))
            ins.then_inc(x2_square, 1)
            pe.wait_ge(yn_ready, C)
            for a in range(NT):
                for half in range(2):
                    for q in range(4):
                        c = 4 * half + q
                        ins = nc.tensor.transpose(bank[1 + 2 * a + half][0:TT, q * P:(q + 1) * P],
                                                  yT[:, c, a * TT:(a + 1) * TT], ident[:, :])
                    ins.then_inc(y_full, 1)


_INS = ["x_prompt", "x_sample", "c_prompt", "c_sample", "state_conv_a", "state_conv_b", "state_pool", "w_ada", "b_ada",
        "norm_mix_g", "w_in", "conv_a_w", "conv_b_w", "conv_b_bias", "ln_b_g", "ln_b_b", "pool_w", "pool_scale",
        "w_out", "norm_ffn_g", "w_router", "router_bias", "w_gate", "w_up", "w_down", "ws_gate", "ws_up", "ws_down",
        "final_norm_g"]
_OUTS = [(1, SEQ, D), (NSEQ, STEPS, D), (1, 1, SA, DA), (1, 1, SB, DB), (1, 1, SP, DC),
         (1, NSEQ, SA, DA), (1, NSEQ, SB, DB), (1, NSEQ, SP, DC)]


def kernel(**inputs):
    import numpy as np
    import concourse.bacc as bacc
    from concourse.bass_utils import run_bass_kernel_spmd

    nc = bacc.Bacc("TRN2", target_bir_lowering=False, num_devices=1)
    arrays, args = {}, []
    for name in _INS:
        a = np.ascontiguousarray(inputs[name])
        arrays[f"in_{name}"] = a
        args.append(nc.dram_tensor(f"in_{name}", a.shape, mybir.dt.from_np(a.dtype), kind="ExternalInput").ap())
    for i, shape in enumerate(_OUTS):
        args.append(nc.dram_tensor(f"out_{i}", shape, F32, kind="ExternalOutput").ap())
    layer(nc, *args)
    r = run_bass_kernel_spmd(nc, [arrays], core_ids=[0])
    return tuple(r.results[0][f"out_{i}"] for i in range(len(_OUTS)))
```
